# Optimizing a Trainium2 kernel written in Bass

```python
import jax
import jax.numpy as jnp
from jax import lax
import numpy as np

D_MODEL = 2048
BATCH = 1
SEQ = 512
DEPTH = 1

N_MIXERS = 4
HEAD_DIM = 128
N_HEADS = D_MODEL // HEAD_DIM
D_FF = 4 * D_MODEL
EPS = 1e-6
NEG = -1e30
BIG = 1e4
CONV_WIDTH = 3
NSA_KV_GROUPS = 4
NSA_HPG = N_HEADS // NSA_KV_GROUPS
CMP_LEN = 32
CMP_STRIDE = 16
SEL_LEN = 64
SEL_TOPK = 16
WINDOW = 512
Q_BLOCK = 128
SEL_Q_CHUNK = 64
POOL_WINDOWS = (2, 4, 8, 16)
POOL_GROUP = D_MODEL // len(POOL_WINDOWS)
NSA_IN_WIDTH = N_HEADS * HEAD_DIM + 6 * NSA_KV_GROUPS * HEAD_DIM + 3 * N_HEADS

kernel_name = 'hybrid_interleaved_conv_nsa_pool_stickbreak'

def rmsnorm(x, g):
    xf = x.astype(jnp.float32)
    y = xf * lax.rsqrt(jnp.mean(xf * xf, axis=-1, keepdims=True) + EPS)
    return (y * g.astype(jnp.float32)).astype(x.dtype)

def short_conv_mixer(h, w_in, conv_w, w_out):
    d = h.shape[-1]
    b_gate, c_gate, v = jnp.split(h @ w_in, 3, axis=-1)
    u = c_gate * v
    y = lax.conv_general_dilated(
        u, conv_w[:, None, :].astype(u.dtype), window_strides=(1,),
        padding=[(CONV_WIDTH - 1, 0)], dimension_numbers=('NWC', 'WIO', 'NWC'),
        feature_group_count=d)
    return (b_gate * y) @ w_out

def _compress(t, pos, w1, w2):
    bsz, seq, g, dh = t.shape
    n_c = (seq - CMP_LEN) // CMP_STRIDE + 1
    r = CMP_LEN // CMP_STRIDE
    chunks = t.reshape(bsz, seq // CMP_STRIDE, CMP_STRIDE, g, dh)
    blocks = jnp.concatenate([chunks[:, j:j + n_c] for j in range(r)], axis=2)
    blocks = blocks + pos[:, None, :].astype(t.dtype)
    flat = jnp.moveaxis(blocks, 3, 2).reshape(bsz, n_c, g, CMP_LEN * dh)
    return jax.nn.silu(flat @ w1) @ w2

def nsa_mixer(h, w_in, q_gain, k_gain, cmp_pos, cmp_w1, cmp_w2, w_out):
    bsz, seq, _ = h.shape
    H, G, hpg, dh = N_HEADS, NSA_KV_GROUPS, NSA_HPG, HEAD_DIM
    dt = h.dtype
    scale = dh ** -0.5
    offs = [int(o) for o in np.cumsum([H * dh] + [G * dh] * 6)]
    q, kc, vc, ks, vs, kw, vw, gates = jnp.split(h @ w_in, offs, axis=-1)
    q = rmsnorm(q.reshape(bsz, seq, G, hpg, dh), q_gain)
    pos_q = jnp.arange(seq)

    kcc = rmsnorm(_compress(kc.reshape(bsz, seq, G, dh), cmp_pos[0], cmp_w1[0], cmp_w2[0]), k_gain[0])
    vcc = _compress(vc.reshape(bsz, seq, G, dh), cmp_pos[1], cmp_w1[1], cmp_w2[1])
    n_c = kcc.shape[1]
    c_end = jnp.arange(n_c) * CMP_STRIDE + CMP_LEN - 1
    c_valid = (c_end[None, :] <= pos_q[:, None])[None, :, None, None, :]
    s_c = jnp.einsum('bqghd,bcgd->bqghc', q, kcc).astype(jnp.float32) * scale
    p_c = jnp.where(c_valid, jax.nn.softmax(jnp.where(c_valid, s_c, NEG), axis=-1), 0.0)
    o_cmp = jnp.einsum('bqghc,bcgd->bqghd', p_c.astype(dt), vcc)

    n_s = seq // SEL_LEN
    ci = np.arange(n_c)[:, None]
    sj = np.arange(n_s)[None, :]
    overlap = ((ci * CMP_STRIDE < (sj + 1) * SEL_LEN) &
               (ci * CMP_STRIDE + CMP_LEN > sj * SEL_LEN)).astype(np.float32)
    imp = jnp.einsum('bqgc,cs->bqgs', p_c.sum(axis=3), jnp.asarray(overlap))
    blk = jnp.arange(n_s)[None, :]
    cur = (pos_q // SEL_LEN)[:, None]
    forced = ((blk == 0) | (blk == cur) | (blk == cur - 1))[:, None, :]
    blk_valid = (blk * SEL_LEN <= pos_q[:, None])[:, None, :]
    imp = jnp.where(forced, BIG, jnp.where(blk_valid, imp, -BIG))
    k_top = min(SEL_TOPK, n_s)
    _, idx = lax.top_k(imp, k_top)

    ks_b = rmsnorm(ks.reshape(bsz, seq, G, dh), k_gain[1]).reshape(bsz, n_s, SEL_LEN, G, dh).transpose(0, 3, 1, 2, 4)
    vs_b = vs.reshape(bsz, n_s, SEL_LEN, G, dh).transpose(0, 3, 1, 2, 4)
    n_q = seq // SEL_Q_CHUNK
    q_ch = q.reshape(bsz, n_q, SEL_Q_CHUNK, G, hpg, dh).swapaxes(0, 1)
    idx_ch = idx.reshape(bsz, n_q, SEL_Q_CHUNK, G, k_top).swapaxes(0, 1)
    pos_ch = pos_q.reshape(n_q, SEL_Q_CHUNK)
    bi = jnp.arange(bsz)[:, None, None, None]
    gi = jnp.arange(G)[None, None, :, None]
    lane = jnp.arange(SEL_LEN)

    def sel_chunk(args):
        qc, ic, pc = args
        kg = ks_b[bi, gi, ic]
        vg = vs_b[bi, gi, ic]
        s = jnp.einsum('bcghd,bcgkld->bcghkl', qc, kg).astype(jnp.float32) * scale
        kpos = ic[..., None] * SEL_LEN + lane
        valid = (kpos <= pc[None, :, None, None, None])[:, :, :, None]
        s = jnp.where(valid, s, NEG)
        sh = s.shape
        p = jax.nn.softmax(s.reshape(sh[:4] + (sh[4] * sh[5],)), axis=-1).reshape(sh)
        return jnp.einsum('bcghkl,bcgkld->bcghd', p.astype(dt), vg)

    o_sel = lax.map(sel_chunk, (q_ch, idx_ch, pos_ch)).swapaxes(0, 1).reshape(bsz, seq, G, hpg, dh)

    nb = seq // Q_BLOCK
    nw = WINDOW // Q_BLOCK
    kwn = rmsnorm(kw.reshape(bsz, seq, G, dh), k_gain[2])
    kp = jnp.pad(kwn, ((0, 0), (WINDOW, 0), (0, 0), (0, 0))).reshape(bsz, nb + nw, Q_BLOCK, G, dh)
    vp = jnp.pad(vw.reshape(bsz, seq, G, dh), ((0, 0), (WINDOW, 0), (0, 0), (0, 0))).reshape(bsz, nb + nw, Q_BLOCK, G, dh)
    k_band = jnp.concatenate([kp[:, j:j + nb] for j in range(nw + 1)], axis=2)
    v_band = jnp.concatenate([vp[:, j:j + nb] for j in range(nw + 1)], axis=2)
    qpos = jnp.arange(nb)[:, None] * Q_BLOCK + jnp.arange(Q_BLOCK)[None, :]
    kpos = jnp.arange(nb)[:, None] * Q_BLOCK - WINDOW + jnp.arange((nw + 1) * Q_BLOCK)[None, :]
    w_valid = ((kpos[:, None, :] <= qpos[:, :, None]) & (qpos[:, :, None] - kpos[:, None, :] < WINDOW)
               & (kpos[:, None, :] >= 0))[None, :, :, None, None, :]
    qb = q.reshape(bsz, nb, Q_BLOCK, G, hpg, dh)
    s_w = jnp.einsum('bnqghd,bnkgd->bnqghk', qb, k_band).astype(jnp.float32) * scale
    p_w = jax.nn.softmax(jnp.where(w_valid, s_w, NEG), axis=-1)
    o_win = jnp.einsum('bnqghk,bnkgd->bnqghd', p_w.astype(dt), v_band).reshape(bsz, seq, G, hpg, dh)

    g = jax.nn.sigmoid(gates.astype(jnp.float32)).astype(dt).reshape(bsz, seq, G, hpg, 3)
    o = g[..., 0:1] * o_cmp + g[..., 1:2] * o_sel + g[..., 2:3] * o_win
    return o.reshape(bsz, seq, H * dh) @ w_out

def pool_mixer(h, w_grp, scale):
    bsz, seq, d = h.shape
    n_g = len(POOL_WINDOWS)
    hg = h.reshape(bsz, seq, n_g, POOL_GROUP).astype(jnp.float32)
    c0 = jnp.concatenate([jnp.zeros((bsz, 1, n_g, POOL_GROUP), jnp.float32), jnp.cumsum(hg, axis=1)], axis=1)
    win = jnp.array(POOL_WINDOWS)[None, :]
    pos = jnp.arange(seq)[:, None]
    lo = jnp.maximum(pos + 1 - win, 0)
    cnt = jnp.minimum(pos + 1, win).astype(jnp.float32)
    lower = c0[:, lo, jnp.arange(n_g)[None, :]]
    pooled = (c0[:, 1:] - lower) / cnt[None, :, :, None] - hg
    y = jnp.einsum('bsgc,gce->bsge', pooled.astype(h.dtype), w_grp).reshape(bsz, seq, d)
    return y * scale

def stick_breaking_mixer(h, w_in, q_gain, k_gain, w_out):
    bsz, seq, _ = h.shape
    H, dh = N_HEADS, HEAD_DIM
    q, k, v = jnp.split(h @ w_in, 3, axis=-1)
    q = rmsnorm(q.reshape(bsz, seq, H, dh), q_gain)
    k = rmsnorm(k.reshape(bsz, seq, H, dh), k_gain)
    v = v.reshape(bsz, seq, H, dh)
    nb = seq // Q_BLOCK
    qb = q.reshape(bsz, nb, Q_BLOCK, H, dh).swapaxes(0, 1)
    kpos = jnp.arange(seq)
    scale = dh ** -0.5

    def block(args):
        qc, i = args
        qpos = i * Q_BLOCK + jnp.arange(Q_BLOCK)
        z = jnp.einsum('bqhd,bkhd->bhqk', qc, k).astype(jnp.float32) * scale
        before = kpos[None, :] < qpos[:, None]
        log_1m = jnp.where(before, jax.nn.log_sigmoid(-z), 0.0)
        tail = lax.cumsum(log_1m, axis=3, reverse=True) - log_1m
        a = jnp.where(before, jnp.exp(jax.nn.log_sigmoid(z) + tail), 0.0)
        return jnp.einsum('bhqk,bkhd->bqhd', a.astype(v.dtype), v)

    o = lax.map(block, (qb, jnp.arange(nb))).swapaxes(0, 1).reshape(bsz, seq, H * dh)
    return o @ w_out

def squared_relu_mlp(h, w1, w2):
    a = jax.nn.relu(h @ w1)
    return (a * a) @ w2

def _n_layers_of(kind):
    return len(range(kind, DEPTH, N_MIXERS))

def setup_inputs(seed: int = 0) -> dict:
    key = jax.random.key(seed)
    ks = iter(jax.random.split(key, 32))
    f32 = jnp.float32
    D, dh, L = D_MODEL, HEAD_DIM, CMP_LEN
    nA, nB, nC, nD = (_n_layers_of(kd) for kd in range(N_MIXERS))

    def nrm(shape, fan_in, mult=1.0):
        return jax.random.normal(next(ks), shape, f32) * (mult * fan_in ** -0.5)

    def gain(shape):
        return 1.0 + 0.05 * jax.random.normal(next(ks), shape, f32)

    return {
        'x': jax.random.normal(next(ks), (BATCH, SEQ, D), f32),
        'mix_norm': gain((DEPTH, D)),
        'mlp_norm': gain((DEPTH, D)),
        'mlp_w1': nrm((DEPTH, D, D_FF), D),
        'mlp_w2': nrm((DEPTH, D_FF, D), D_FF),
        'conv_w_in': nrm((nA, D, 3 * D), D),
        'conv_w': nrm((nA, CONV_WIDTH, D), CONV_WIDTH),
        'conv_w_out': nrm((nA, D, D), D),
        'nsa_w_in': nrm((nB, D, NSA_IN_WIDTH), D),
        'nsa_q_gain': gain((nB, dh)),
        'nsa_k_gain': gain((nB, 3, dh)),
        'nsa_cmp_pos': 0.5 * jax.random.normal(next(ks), (nB, 2, L, dh), f32),
        'nsa_cmp_w1': nrm((nB, 2, L * dh, dh), L * dh),
        'nsa_cmp_w2': nrm((nB, 2, dh, dh), dh),
        'nsa_w_out': nrm((nB, N_HEADS * dh, D), N_HEADS * dh),
        'pool_w': nrm((nC, len(POOL_WINDOWS), POOL_GROUP, POOL_GROUP), POOL_GROUP),
        'pool_scale': gain((nC, D)),
        'sb_w_in': nrm((nD, D, 3 * N_HEADS * dh), D),
        'sb_q_gain': gain((nD, dh)),
        'sb_k_gain': gain((nD, dh)),
        'sb_w_out': nrm((nD, N_HEADS * dh, D), N_HEADS * dh),
    }

def reference(x, mix_norm, mlp_norm, mlp_w1, mlp_w2, conv_w_in, conv_w, conv_w_out,
              nsa_w_in, nsa_q_gain, nsa_k_gain, nsa_cmp_pos, nsa_cmp_w1, nsa_cmp_w2, nsa_w_out,
              pool_w, pool_scale, sb_w_in, sb_q_gain, sb_k_gain, sb_w_out):
    for i in range(DEPTH):
        kind, j = i % N_MIXERS, i // N_MIXERS
        h = rmsnorm(x, mix_norm[i])
        if kind == 0:
            y = short_conv_mixer(h, conv_w_in[j], conv_w[j], conv_w_out[j])
        elif kind == 1:
            y = nsa_mixer(h, nsa_w_in[j], nsa_q_gain[j], nsa_k_gain[j], nsa_cmp_pos[j],
                          nsa_cmp_w1[j], nsa_cmp_w2[j], nsa_w_out[j])
        elif kind == 2:
            y = pool_mixer(h, pool_w[j], pool_scale[j])
        else:
            y = stick_breaking_mixer(h, sb_w_in[j], sb_q_gain[j], sb_k_gain[j], sb_w_out[j])
        x = x + y
        x = x + squared_relu_mlp(rmsnorm(x, mlp_norm[i]), mlp_w1[i], mlp_w2[i])
    return x


_drawn_inputs = setup_inputs


def setup_inputs(seed=0):
    import zlib

    import numpy as np

    out = dict(_drawn_inputs(seed))
    spreads = {}
    factors = {}
    for name, (base, spread) in spreads.items():
        noise = np.random.default_rng([zlib.crc32(name.encode()), seed]).standard_normal(out[name].shape)
        drawn = base * np.exp(spread * noise) if base else spread * noise
        out[name] = jnp.asarray(drawn.astype(out[name].dtype))
    for name, factor in factors.items():
        out[name] = (out[name] * factor).astype(out[name].dtype)
    return out
```

```python
from contextlib import ExitStack

import concourse.bass as bass
from concourse import mybir

P = 128
F32 = mybir.dt.float32
F32R = mybir.dt.float32r
ALU = mybir.AluOpType
ACT = mybir.ActivationFunctionType
AX = mybir.AxisListType

EPS = 1e-6
KT = 16
BW = 512
NT = BW // P
RING = 4
GRAN = 4
TAKE_AT = (4, 7, 10, 13)
NRAW = 2


def conv_mlp_layer(nc, x, mix_norm, mlp_norm, w1, w2, conv_w_in, conv_w, conv_w_out, out):
    S, D = x.shape
    FF = w1.shape[1]
    CW = conv_w.shape[0]
    MT = S // P
    DT = D // P
    NQ = D // BW
    NC = FF // D
    assert S == BW and DT == KT and MT == NT and CW == 3 and NQ == 4

    IN0 = 0
    OUT0 = IN0 + 3 * NQ
    MLP0 = OUT0 + NQ
    NB = MLP0 + 2 * NQ * NC

    x_v = x.rearrange("(m p) d -> p m d", p=P)
    out_v = out.rearrange("(m p) d -> p m d", p=P)
    w_in_v = conv_w_in.rearrange("(k p) n -> p k n", p=P)
    w_out_v = conv_w_out.rearrange("(k p) n -> p k n", p=P)
    w1_v = w1.rearrange("(k p) n -> p k n", p=P)
    w2_v = w2.rearrange("(k p) n -> p k n", p=P)

    with ExitStack() as ctx:
        def sb(name, shape, dt):
            return ctx.enter_context(nc.sbuf_tensor(name, shape, dt))

        def sem(name):
            return ctx.enter_context(nc.semaphore(name))

        resid = sb("resid", [P, MT, D], F32)
        h_hi = sb("h_hi", [P, DT, S], F32R)
        h_lo = sb("h_lo", [P, DT, S], F32R)
        z_hi = sb("z_hi", [P, KT, S], F32R)
        z_lo = sb("z_lo", [P, KT, S], F32R)
        w_raw = sb("w_raw", [P, NRAW, GRAN, BW], F32)
        w_hi = sb("w_hi", [P, RING, BW], F32R)
        w_lo = sb("w_lo", [P, RING, BW], F32R)
        u_pad = sb("u_pad", [P, NT, CW - 1 + S], F32)
        tmp = sb("tmp", [P, 2, S], F32)
        rstd_b = sb("rstd_b", [P, S], F32)
        ident = sb("ident", [P, P], F32)
        cols = sb("cols", [P, (2 + CW) * DT], F32)
        sumsq = sb("sumsq", [P, MT, NQ], F32)
        stat = sb("stat", [P, 5, MT], F32)
        var, root, r0, r1, rstd = (stat[:, i, :] for i in range(5))
        ones = tmp[:, 0, 0:P]
        diag = tmp[:, 1, :].rearrange("p (m t) -> p m t", t=P)
        squares = tmp[:].rearrange("p a s -> p (a s)")
        rows = u_pad[:, 0, 0:P]
        NR = (2 + CW) * DT
        ps = [ctx.enter_context(nc.psum_tensor(f"ps{i}", [P, BW], F32)) for i in range(2 * NT)]

        x_in = [sem(f"x_in{m}") for m in range(MT)]
        rows_in = [sem(f"rows_in{i}") for i in range(3)]
        first_in = [sem(f"first_in{k}") for k in range(GRAN)]
        raw_in = [sem(f"raw_in{i}") for i in range(NRAW)]
        w_hi_ready = sem("w_hi_ready")
        w_lo_ready = sem("w_lo_ready")
        w_used = sem("w_used")
        last_tile = sem("last_tile")
        bank_free = sem("bank_free")
        z_ready = sem("z_ready")
        turned = sem("turned")
        h_hi_ready = sem("h_hi_ready")
        h_lo_ready = sem("h_lo_ready")
        squared = sem("squared")
        var_ready = sem("var_ready")
        root_ready = sem("root_ready")
        diag_ready = sem("diag_ready")
        spread = sem("spread")
        rstd_ready = sem("rstd_ready")
        ident0 = sem("ident0")
        ident_ready = sem("ident_ready")
        cols_turned = sem("cols_turned")
        cols_ready = sem("cols_ready")
        summed = sem("summed")
        newton = sem("newton")
        conv_step = sem("conv_step")
        relu_step = sem("relu_step")
        u_ready = sem("u_ready")
        stored = sem("stored")

        mix_gain = cols[:, 0:DT]
        mlp_gain = cols[:, DT:2 * DT]

        block = ctx.enter_context(nc.Block())

        @block.sync
        def _(sp):
            def load_first(k):
                sp.dma_start(w_raw[:, 0, k, :], w_in_v[:, k, D:D + BW]).then_inc(first_in[k], 16)

            for m in range(MT):
                if m == MT - 1:
                    load_first(0)
                sp.dma_start(resid[:, m, :], x_v[:, m, :]).then_inc(x_in[m], 16)

            def load_block(b, view, k0, c0, free=True):
                for g in range(KT // GRAN):
                    if not free and g == 0:
                        for k in range(1, GRAN):
                            load_first(k)
                        continue
                    tile = view[:, bass.ds(k0 + GRAN * g, GRAN), bass.ds(c0, BW)]
                    if not isinstance(b, int):
                        tile = bass.AP(tile.tensor, sp.snap(tile.offset), tile.ap)
                    if free or g >= NRAW:
                        sp.wait_ge(w_lo_ready, KT * b + GRAN * (g + 1 - NRAW))
                    sp.dma_start(w_raw[:, g % NRAW, :, :], tile).then_inc(raw_in[g % NRAW], 16)

            for q in range(NQ):
                for j, part in enumerate((1, 2, 0)):
                    load_block(IN0 + 3 * q + j, w_in_v, 0, D * part + BW * q, free=q + j > 0)
            with sp.Fori(0, NQ) as n:
                load_block(OUT0 + n, w_out_v, 0, BW * n)
            with sp.Fori(0, NC) as c:
                with sp.Fori(0, NQ) as j:
                    load_block(MLP0 + 2 * NQ * c + j, w1_v, 0, D * c + BW * j)
                with sp.Fori(0, NQ) as n:
                    load_block(MLP0 + 2 * NQ * c + NQ + n, w2_v, KT * c, BW * n)

            for n in range(NQ):
                for m in range(MT):
                    sp.wait_ge(bank_free, NT * (NB - NQ + n) + m + 1)
                    sp.dma_start(out_v[:, m, BW * n:BW * (n + 1)],
                                 resid[:, m, BW * n:BW * (n + 1)]).then_inc(stored, 16)
            sp.wait_ge(stored, 16 * NQ * MT)

        @block.gpsimd
        def _(pool):
            nc.gpsimd.memset(ident[:], 0.0).then_inc(ident0, 1)
            pool.wait_ge(ident0, 1)
            nc.gpsimd.affine_select(out=ident[:], in_=ident[:], compare_op=ALU.not_equal, fill=1.0, base=0,
                                    pattern=[[-1, P]], channel_multiplier=1).then_inc(ident_ready, 1)

        @block.scalar
        def _(act):
            def split_hi(b, k, first=False):
                if first and k < GRAN:
                    act.wait_ge(first_in[k], 16)
                elif k % GRAN == 0:
                    slot = k // GRAN % NRAW
                    act.wait_ge(raw_in[slot], 16 * (b * (KT // GRAN // NRAW) + (k // (GRAN * NRAW) + (slot > 0))))
                if not first or k >= RING:
                    act.wait_ge(w_used, KT * b + k + 1 - RING)
                nc.scalar.activation(w_hi[:, k % RING, :], w_raw[:, k // GRAN % NRAW, k % GRAN, :],
                                     ACT.Copy).then_inc(w_hi_ready, 1)

            squares_done = [0]

            def square(m, n, width):
                if squares_done[0]:
                    act.wait_ge(squared, squares_done[0])
                squares_done[0] += 1
                at = slice(width * n, width * (n + 1))
                nc.scalar.activation(squares[:, 0:width], resid[:, m, at], ACT.Square,
                                     accum_out=sumsq[:, m, n:n + 1]).then_inc(squared, 1)

            def h_part(kk, done, gain, bk):
                act.wait_ge(turned, done)
                nc.scalar.activation(h_hi[:, kk, :], ps[bk][:], ACT.Copy,
                                     scale=gain[:, kk:kk + 1]).then_inc(h_hi_ready, 1)

            act.dma_start(rows[0:DT, :], mix_norm.rearrange("(k p) -> k p", p=P)).then_inc(rows_in[0], 16)
            act.dma_start(rows[DT:2 * DT, :], mlp_norm.rearrange("(k p) -> k p", p=P)).then_inc(rows_in[1], 16)
            act.dma_start(rows[2 * DT:NR, :], conv_w.rearrange("j (k p) -> (j k) p", p=P)).then_inc(rows_in[2], 16)

            for m in range(MT - 1):
                act.wait_ge(x_in[m], 16)
                square(m, 0, D // 2)
                square(m, 1, D // 2)
            act.wait_ge(cols_ready, 1)
            for k in range(KT):
                split_hi(0, k, first=True)
                h_part(k, k + 1, mix_gain, NT + k % NT)
                if k == 2:
                    act.wait_ge(x_in[MT - 1], 16)
                    square(MT - 1, 0, D // 2)
                    square(MT - 1, 1, D // 2)
                if k == 6:
                    act.wait_ge(var_ready, 1)
                    nc.scalar.activation(root, var, ACT.Sqrt).then_inc(root_ready, 1)
            with act.Fori(1, OUT0 + 1) as b:
                for k in range(KT):
                    split_hi(b, k)
            for n in range(NQ):
                b = OUT0 + 1 + n
                last = n == NQ - 1
                for k in range(KT):
                    split_hi(b, k)
                    m = k - (6 if last else 8)
                    if 0 <= m < MT:
                        act.wait_ge(bank_free, NT * (b - 1) + m + 1)
                        square(m, n, BW)
                    j = k - (8 if last else 11)
                    if 0 <= j < NT:
                        h_part(NT * n + j, DT + NT * n + j + 1, mlp_gain, NT * ((b - 1) % 2) + j)
                    if last and k == 13:
                        act.wait_ge(var_ready, 2)
                        nc.scalar.activation(root, var, ACT.Sqrt).then_inc(root_ready, 1)
            with act.Fori(MLP0 + 1, NB) as b:
                for k in range(KT):
                    split_hi(b, k)

        @block.vector
        def _(dve):
            def link(ins, on, value):
                ins.then_inc(on, 1)
                dve.wait_ge(on, value)

            def split_lo(b, k):
                dve.wait_ge(w_hi_ready, KT * b + k + 1)
                nc.vector.tensor_tensor(w_lo[:, k % RING, :], w_raw[:, k // GRAN % NRAW, k % GRAN, :],
                                        w_hi[:, k % RING, :].bitcast(F32), ALU.subtract).then_inc(w_lo_ready, 1)

            def h_part(kk, done, gain, bk):
                dve.wait_ge(h_hi_ready, done)
                nc.vector.scalar_tensor_tensor(out=h_lo[:, kk, :], in0=ps[bk][:], scalar=gain[:, kk:kk + 1],
                                               in1=h_hi[:, kk, :].bitcast(F32), op0=ALU.mult,
                                               op1=ALU.subtract).then_inc(h_lo_ready, 1)

            def mean_square(n, parts, done):
                dve.wait_ge(squared, done)
                link(nc.vector.tensor_reduce(rstd, sumsq[:, :, 0:parts], AX.X, ALU.add), summed, n)
                nc.vector.tensor_scalar(var, rstd, 1.0 / D, EPS, ALU.mult, ALU.add).then_inc(var_ready, 1)
                nc.vector.memset(ones, 1.0)

            def rstd_diagonals(n):
                dve.wait_ge(root_ready, n)
                link(nc.vector.reciprocal(r0, root), newton, 5 * n - 4)
                link(nc.vector.tensor_tensor(r1, r0, r0, ALU.mult), newton, 5 * n - 3)
                link(nc.vector.tensor_tensor(r1, r1, var, ALU.mult), newton, 5 * n - 2)
                link(nc.vector.tensor_scalar(r1, r1, -0.5, 1.5, ALU.mult, ALU.add), newton, 5 * n - 1)
                link(nc.vector.tensor_tensor(rstd, r0, r1, ALU.mult), newton, 5 * n)
                for m in range(MT):
                    ins = nc.vector.tensor_scalar(diag[:, m, :], ident[:], rstd[:, m:m + 1], None, ALU.mult)
                ins.then_inc(diag_ready, 1)

            def rstd_copy(n):
                dve.wait_ge(spread, n)
                nc.vector.tensor_copy(rstd_b[:], ps[NT][:]).then_inc(rstd_ready, 1)

            def take_c(b, i, bk, q):
                nc.vector.tensor_tensor(u_pad[:, i, CW - 1:], bk, rstd_b[:], ALU.mult).then_inc(bank_free, 1)

            def take_v(b, i, bk, q):
                link(nc.vector.tensor_tensor(tmp[:, 0, :], bk, rstd_b[:], ALU.mult), bank_free, NT * b + (i + 1))
                link(nc.vector.tensor_tensor(u_pad[:, i, CW - 1:], u_pad[:, i, CW - 1:], tmp[:, 0, :], ALU.mult),
                     u_ready, NT * q + (i + 1))

            def split_z(value, idx, on, count, ready):
                link(nc.vector.tensor_copy(z_hi[:, bass.ds(idx, 1), :], value), on, count)
                link(nc.vector.tensor_tensor(z_lo[:, bass.ds(idx, 1), :], value,
                                             z_hi[:, bass.ds(idx, 1), :].bitcast(F32), ALU.subtract), z_ready, ready)

            def take_b(b, i, bk, q):
                done = 5 * NT * q + 5 * i
                t, y = tmp[:, 0, :], tmp[:, 1, :]

                def taps(j):
                    return cols[:, bass.ds(NT * q + ((2 + j) * DT + i), 1)]

                link(nc.vector.tensor_tensor(t, bk, rstd_b[:], ALU.mult), bank_free, NT * b + (i + 1))
                link(nc.vector.tensor_scalar(y, u_pad[:, i, 0:S], taps(0), None, ALU.mult), conv_step, done + 1)
                for j in (1, 2):
                    link(nc.vector.scalar_tensor_tensor(out=y, in0=u_pad[:, i, j:j + S], scalar=taps(j), in1=y,
                                                        op0=ALU.mult, op1=ALU.add), conv_step, done + (1 + j))
                link(nc.vector.tensor_tensor(y, y, t, ALU.mult), conv_step, done + 4)
                split_z(tmp[:, 1:2, :], NT * q + i, conv_step, done + 5, NT * q + (i + 1))

            def take_up(b, i, bk, c, j):
                done = 2 * KT * c + (2 * NT * j + 2 * i)
                link(nc.vector.tensor_tensor(tmp[:, 0, :], bk, rstd_b[:], ALU.mult), bank_free, NT * b + (i + 1))
                link(nc.vector.scalar_tensor_tensor(out=tmp[:, 1, :], in0=tmp[:, 0, :], scalar=0.0, in1=tmp[:, 0, :],
                                                    op0=ALU.max, op1=ALU.mult), relu_step, done + 1)
                split_z(tmp[:, 1:2, :], NT * j + i, relu_step, done + 2, KT * c + (NT * j + (KT + i + 1)))

            def take_resid(m, bk, n):
                at = resid[:, m, bass.ds(BW * n, BW)]
                nc.vector.tensor_tensor(at, bk, at, ALU.add).then_inc(bank_free, 1)

            def block_step(b, parity, take):
                for k in range(KT):
                    split_lo(b + 1, k)
                    if k in TAKE_AT:
                        i = TAKE_AT.index(k)
                        if i == 0:
                            dve.wait_ge(w_used, KT * (b + 1))
                        take(i, ps[NT * parity + i][:])

            dve.wait_ge(cols_turned, 1)
            nc.vector.tensor_copy(cols[:], ps[0][:, 0:NR]).then_inc(cols_ready, 1)
            nc.vector.memset(u_pad[:, :, 0:CW - 1], 0.0)
            dve.wait_ge(cols_ready, 1)

            for k in range(KT):
                split_lo(0, k)
                h_part(k, k + 1, mix_gain, NT + k % NT)
                if k == 5:
                    mean_square(1, 2, 2 * MT)
                if k == 7:
                    rstd_diagonals(1)
            rstd_copy(1)

            with dve.Fori(0, NQ // 2) as two:
                for sub in range(2):
                    for t, take in enumerate((take_c, take_v, take_b)):
                        q = 2 * two + sub
                        b = 6 * two + (3 * sub + t)
                        block_step(b, (3 * sub + t) % 2, lambda i, bk: take(b, i, bk, q))

            for n in range(NQ):
                b = OUT0 + n
                last = n == NQ - 1
                for k in range(KT):
                    split_lo(b + 1, k)
                    if k == 4:
                        dve.wait_ge(w_used, KT * (b + 1))
                    for m in range(MT):
                        if k == (4 + m // 2 if last else 4 + m):
                            take_resid(m, ps[NT * (b % 2) + m][:], n)
                    j = k - (9 if last else 12)
                    if 0 <= j < NT:
                        h_part(NT * n + j, DT + NT * n + j + 1, mlp_gain, NT * (b % 2) + j)
                    if last and k == 12:
                        mean_square(2, NQ, 2 * MT + MT * NQ)
                    if last and k == 13:
                        rstd_diagonals(2)
            rstd_copy(2)

            def up_pair(c, half):
                for sub in range(2):
                    j = 2 * half + sub
                    b = 2 * NQ * c + (2 * half + (MLP0 + sub))
                    block_step(b, sub, lambda i, bk: take_up(b, i, bk, c, j))

            def down_step(c, n, sub):
                b = 2 * NQ * c + (n + (MLP0 + NQ))
                block_step(b, sub, lambda i, bk: take_resid(i, bk, n))

            def down_pair(c, half):
                for sub in range(2):
                    down_step(c, 2 * half + sub, sub)

            with dve.Fori(0, NC - 1) as c:
                with dve.Fori(0, NQ // 2) as half:
                    up_pair(c, half)
                with dve.Fori(0, NQ // 2) as half:
                    down_pair(c, half)
            with dve.Fori(0, NQ // 2) as half:
                up_pair(NC - 1, half)
            down_pair(NC - 1, 0)
            down_step(NC - 1, NQ - 2, 0)
            for m in range(MT):
                dve.wait_ge(last_tile, m + 1)
                take_resid(m, ps[NT + m][:], NQ - 1)

        @block.tensor
        def _(pe):
            def pe_loop(start, end):
                return nc.Fori(start, end, engines=[mybir.EngineType.PE], hint_back_edge=True)

            def turn_tile(kk, bk, m):
                return nc.tensor.transpose(ps[bk][:, P * m:P * (m + 1)], resid[:, m, P * kk:P * (kk + 1)], ident[:])

            def turn(kk, bk):
                for m in range(MT):
                    mm = turn_tile(kk, bk, m)
                mm.then_inc(turned, 1)

            def spread_rstd(n):
                pe.wait_ge(diag_ready, n)
                for m in range(MT):
                    mm = nc.tensor.matmul(ps[NT][:, P * m:P * (m + 1)], ones, diag[:, m, :], start=True, stop=True)
                mm.then_inc(spread, 1)

            def tile_products(k, i, parity, act_moving):
                part = slice(P * i, P * (i + 1))
                whi, wlo = w_hi[:, k % RING, :], w_lo[:, k % RING, :]
                if act_moving:
                    pairs = ((wlo[:, part], h_hi[:, k, :]), (whi[:, part], h_lo[:, k, :]),
                             (whi[:, part], h_hi[:, k, :]))
                else:
                    pairs = ((z_lo[:, k, part], whi), (z_hi[:, k, part], wlo), (z_hi[:, k, part], whi))
                for j, (stationary, moving) in enumerate(pairs):
                    mm = nc.tensor.matmul(ps[NT * parity + i][:], stationary, moving, start=(k == 0 and j == 0),
                                          stop=(k == KT - 1 and j == 2))
                return mm

            def products(b, k, parity, act_moving):
                pe.wait_ge(w_lo_ready, KT * b + (k + 1))
                for i in range(NT):
                    mm = tile_products(k, i, parity, act_moving)
                mm.then_inc(w_used, 1)

            def banks_free(b):
                pe.wait_ge(bank_free, NT * (b - 1))

            def whole_block(b, parity, act_moving):
                banks_free(b)
                for k in range(KT):
                    products(b, k, parity, act_moving)

            for s in rows_in:
                pe.wait_ge(s, 16)
            pe.wait_ge(ident_ready, 1)
            nc.tensor.transpose(ps[0][:, 0:NR], rows[0:NR, :], ident[0:NR, 0:NR]).then_inc(cols_turned, 1)

            for m in range(MT):
                pe.wait_ge(x_in[m], 16)
                for k in range(NT):
                    mm = turn_tile(k, NT + k, m)
                    if m == MT - 1:
                        mm.then_inc(turned, 1)
            pe.wait_ge(cols_ready, 1)
            for k in range(KT):
                pe.wait_ge(h_lo_ready, k + 1)
                products(0, k, 0, True)
                if k + NT < KT:
                    turn(k + NT, NT + k % NT)
                if k == KT - 2:
                    spread_rstd(1)
            pe.wait_ge(rstd_ready, 1)
            for k in range(KT):
                products(1, k, 1, True)
            with pe_loop(1, OUT0 // 2) as two:
                for sub in range(2):
                    whole_block(2 * two + sub, sub, True)

            for n in range(NQ):
                b = OUT0 + n
                banks_free(b)
                if n > 1:
                    pe.wait_ge(h_lo_ready, DT + NT * (n - 1))
                for k in range(KT):
                    if n == 0:
                        pe.wait_ge(z_ready, k + 1)
                    if n > 0 and k == 8:
                        pe.wait_ge(bank_free, NT * b)
                        for j in range(NT):
                            turn(NT * (n - 1) + j, NT * ((b - 1) % 2) + j)
                    products(b, k, b % 2, False)

            pe.wait_ge(h_lo_ready, DT + NT * (NQ - 1))
            banks_free(MLP0)
            for k in range(KT):
                if k == 6:
                    pe.wait_ge(bank_free, NT * MLP0)
                    for j in range(NT):
                        turn(NT * (NQ - 1) + j, NT + j)
                pe.wait_ge(h_lo_ready, DT + k + 1)
                products(MLP0, k, 0, True)
                if k == KT - 2:
                    spread_rstd(2)
            pe.wait_ge(rstd_ready, 2)
            whole_block(MLP0 + 1, 1, True)

            def up_half(c, half):
                for sub in range(2):
                    whole_block(2 * NQ * c + (2 * half + (MLP0 + sub)), sub, True)

            def down_half(c, half):
                for sub in range(2):
                    b = 2 * NQ * c + (2 * half + (MLP0 + NQ + sub))
                    banks_free(b)
                    for k in range(KT):
                        if sub == 0:
                            pe.wait_ge(z_ready, KT * (c + 1) + (k + 1))
                        products(b, k, sub, False)

            up_half(0, 1)
            with pe_loop(0, NC - 1) as c:
                with pe_loop(0, NQ // 2) as half:
                    down_half(c, half)
                with pe_loop(0, NQ // 2) as half:
                    up_half(c + 1, half)
            down_half(NC - 1, 0)
            whole_block(NB - 2, 0, False)

            banks_free(NB - 1)
            for k in range(KT - 2):
                products(NB - 1, k, 1, False)
            pe.wait_ge(w_lo_ready, KT * NB)
            for i in range(NT):
                for k in range(KT - 2, KT):
                    mm = tile_products(k, i, 1, False)
                mm.then_inc(last_tile, 1)


_INS = ['x', 'mix_norm', 'mlp_norm', 'mlp_w1', 'mlp_w2', 'conv_w_in', 'conv_w', 'conv_w_out']


def kernel(**inputs):
    import numpy as _np
    import concourse.bacc as _bacc
    from concourse import mybir as _mybir
    from concourse.bass_utils import run_bass_kernel_spmd as _run

    nc = _bacc.Bacc("TRN2", target_bir_lowering=False, num_devices=1)
    arrays, args = {}, []
    for name in _INS:
        a = _np.ascontiguousarray(inputs[name])[0]
        arrays[f"in_{name}"] = a
        args.append(nc.dram_tensor(f"in_{name}", a.shape, _mybir.dt.from_np(a.dtype), kind="ExternalInput").ap())
    shape = inputs['x'].shape
    out = nc.dram_tensor("out", shape[1:], _mybir.dt.float32, kind="ExternalOutput").ap()
    conv_mlp_layer(nc, *args, out)
    r = _run(nc, [arrays], core_ids=[0])
    return r.results[0]["out"].reshape(shape)
```

```python
from contextlib import ExitStack

import concourse.bass as bass
from concourse import mybir

P = 128
F32 = mybir.dt.float32
F32R = mybir.dt.float32r
ALU = mybir.AluOpType
ACT = mybir.ActivationFunctionType

EPS = 1e-6
KT = 16
BW = 512
NT = BW // P
RING = 4
GRAN = 4
NG = KT // GRAN
NRAW = 2
SQUARES_AT = {2: (0,), 3: (1,), 4: (2,), 5: (3, 4), 6: (5,), 7: (6, 7), 8: (8, 9),
              9: (10, 11), 10: (12, 13), 11: (14, 15)}
TAKE_AT = (4, 7, 10, 13)


def conv_mlp_layer(nc, xt, weights, cols_dram, outt, FF):
    D, S = xt.shape
    CW = 3
    DT = D // P
    NQ = D // BW
    NC = FF // D
    OUT0 = 3 * NQ
    MLP0 = OUT0 + NQ
    NB = MLP0 + 2 * NQ * NC
    assert S == BW and DT == KT and NQ == 4 and weights.shape[0] == NG * NB

    xt_v = xt.rearrange("(k p) t -> p k t", p=P)
    outt_v = outt.rearrange("(k p) t -> p k t", p=P)

    with ExitStack() as ctx:
        def sb(name, shape, dt):
            return ctx.enter_context(nc.sbuf_tensor(name, shape, dt))

        def sem(name):
            return ctx.enter_context(nc.semaphore(name))

        resid = sb("resid", [P, DT, S], F32)
        h_hi = sb("h_hi", [P, DT, S], F32R)
        h_lo = sb("h_lo", [P, DT, S], F32R)
        z_hi = sb("z_hi", [P, KT, S], F32R)
        z_lo = sb("z_lo", [P, KT, S], F32R)
        w_raw = sb("w_raw", [P, NRAW, GRAN, BW], F32)
        w_hi = sb("w_hi", [P, RING, BW], F32R)
        w_lo = sb("w_lo", [P, RING, BW], F32R)
        u_pad = sb("u_pad", [P, NT, CW - 1 + S], F32)
        tmp = sb("tmp", [P, 2, S], F32)
        rstd_b = sb("rstd_b", [P, S], F32)
        ones = sb("ones", [P, P], F32)
        cols = sb("cols", [P, (2 + CW) * DT], F32)
        square, square_sum = tmp[:, 0, :], tmp[:, 1, :]
        var, root = tmp[:, 0, :], tmp[:, 1, :]
        ps = [ctx.enter_context(nc.psum_tensor(f"ps{i}", [P, BW], F32)) for i in range(2 * NT)]

        X_PARTS = [(k, 1) for k in range(GRAN)] + [(k, GRAN) for k in range(GRAN, DT, GRAN)]
        x_in = [sem(f"x_in{k}") for k, _ in X_PARTS]
        cols_in = sem("cols_in")
        first_in = [sem(f"first_in{k}") for k in range(GRAN)]
        raw_in = [sem(f"raw_in{i}") for i in range(NRAW)]
        w_hi_ready = sem("w_hi_ready")
        w_lo_ready = sem("w_lo_ready")
        w_used = sem("w_used")
        last_tile = sem("last_tile")
        bank_free = sem("bank_free")
        z_ready = sem("z_ready")
        h_hi_ready = sem("h_hi_ready")
        h_lo_ready = sem("h_lo_ready")
        squared = sem("squared")
        square_added = sem("square_added")
        ones_ready = sem("ones_ready")
        total_ready = sem("total_ready")
        var_ready = sem("var_ready")
        root_ready = sem("root_ready")
        newton = sem("newton")
        conv_step = sem("conv_step")
        relu_step = sem("relu_step")
        u_ready = sem("u_ready")
        pad_ready = sem("pad_ready")
        stored = sem("stored")

        MIX, MLP = 0, DT

        def x_landed(eng, k):
            for s, (first, _) in zip(x_in, X_PARTS):
                if first == k:
                    eng.wait_ge(s, 16)

        block = ctx.enter_context(nc.Block())

        @block.sync
        def _(sp):
            def load_x(k, n):
                s = x_in[X_PARTS.index((k, n))]
                sp.dma_start(resid[:, k:k + n, :], xt_v[:, k:k + n, :]).then_inc(s, 16)

            def load_weights(g, slot):
                sp.dma_start(w_raw[:, slot, :, :],
                             weights[bass.ds(g, 1)].rearrange("a p k n -> p (a k) n")).then_inc(raw_in[slot], 16)

            for k in range(GRAN):
                load_x(k, 1)
                sp.dma_start(w_raw[:, 0, k, :], weights[0, :, k, :]).then_inc(first_in[k], 16)
            load_x(*X_PARTS[GRAN])
            load_weights(1, 1)
            for part in X_PARTS[GRAN + 1:]:
                load_x(*part)
            with sp.Fori(1, NG * NB // NRAW) as turn:
                for slot in range(NRAW):
                    g = NRAW * turn + slot
                    tile = weights[bass.ds(g, 1)].rearrange("a p k n -> p (a k) n")
                    tile = bass.AP(tile.tensor, sp.snap(tile.offset), tile.ap)
                    sp.wait_ge(w_lo_ready, GRAN * NRAW * turn + GRAN * (slot + 1 - NRAW))
                    sp.dma_start(w_raw[:, slot, :, :], tile).then_inc(raw_in[slot], 16)

            for kk in range(DT):
                sp.wait_ge(bank_free, NT * (NB - NQ) + kk + 1)
                sp.dma_start(outt_v[:, kk, :], resid[:, kk, :]).then_inc(stored, 16)
            sp.wait_ge(stored, 16 * DT)

        @block.gpsimd
        def _(pool):
            nc.gpsimd.memset(ones[:], 1.0).then_inc(ones_ready, 1)

        @block.scalar
        def _(act):
            def split_hi(b, k, first=False):
                if first and k < GRAN:
                    act.wait_ge(first_in[k], 16)
                elif k % GRAN == 0:
                    slot = k // GRAN % NRAW
                    act.wait_ge(raw_in[slot], 16 * (b * (NG // NRAW) + (k // (GRAN * NRAW) + (slot > 0))))
                if not first or k >= RING:
                    act.wait_ge(w_used, KT * b + k + 1 - RING)
                nc.scalar.activation(w_hi[:, k % RING, :], w_raw[:, k // GRAN % NRAW, k % GRAN, :],
                                     ACT.Copy).then_inc(w_hi_ready, 1)

            def h_part(kk, gain):
                nc.scalar.activation(h_hi[:, kk, :], resid[:, kk, :], ACT.Copy,
                                     scale=cols[:, gain + kk:gain + kk + 1]).then_inc(h_hi_ready, 1)

            def square_part(kk, norm):
                if kk == 0:
                    o = square_sum
                else:
                    o = square
                    if kk > 1:
                        act.wait_ge(square_added, (DT - 1) * norm + kk - 1)
                nc.scalar.activation(o, resid[:, kk, :], ACT.Square).then_inc(squared, 1)

            def root_of(norm):
                act.wait_ge(var_ready, norm + 1)
                nc.scalar.activation(root, var, ACT.Sqrt).then_inc(root_ready, 1)

            act.dma_start(cols[:], cols_dram).then_inc(cols_in, 16)
            for k in range(KT):
                x_landed(act, k)
                if k == 0:
                    act.wait_ge(cols_in, 16)
                h_part(k, MIX)
                split_hi(0, k, first=True)
                for kk in SQUARES_AT.get(k, ()):
                    square_part(kk, 0)
                if k == 13:
                    root_of(0)
            with act.Fori(1, OUT0 + 1) as b:
                for k in range(KT):
                    split_hi(b, k)
            for n in range(NQ):
                b = OUT0 + 1 + n
                last = n == NQ - 1
                for k in range(KT):
                    split_hi(b, k)
                    i = k - 6
                    if 0 <= i < NT:
                        act.wait_ge(bank_free, NT * (b - 1) + i + 1)
                        h_part(NT * n + i, MLP)
                        square_part(NT * n + i, 1)
                    if last and k == 13:
                        root_of(1)
            with act.Fori(MLP0 + 1, NB) as b:
                for k in range(KT):
                    split_hi(b, k)

        @block.vector
        def _(dve):
            def link(ins, on, value):
                ins.then_inc(on, 1)
                dve.wait_ge(on, value)

            def split_lo(b, k):
                dve.wait_ge(w_hi_ready, KT * b + k + 1)
                nc.vector.tensor_tensor(w_lo[:, k % RING, :], w_raw[:, k // GRAN % NRAW, k % GRAN, :],
                                        w_hi[:, k % RING, :].bitcast(F32), ALU.subtract).then_inc(w_lo_ready, 1)

            def h_part(kk, gain):
                dve.wait_ge(h_hi_ready, gain + kk + 1)
                nc.vector.scalar_tensor_tensor(out=h_lo[:, kk, :], in0=resid[:, kk, :],
                                               scalar=cols[:, gain + kk:gain + kk + 1],
                                               in1=h_hi[:, kk, :].bitcast(F32), op0=ALU.mult,
                                               op1=ALU.subtract).then_inc(h_lo_ready, 1)

            def add_square(kk, norm):
                done = (DT - 1) * norm + kk
                dve.wait_ge(squared, DT * norm + kk + 1)
                if kk > 1:
                    dve.wait_ge(square_added, done - 1)
                nc.vector.tensor_tensor(square_sum, square_sum, square, ALU.add).then_inc(square_added, 1)

            def variance(norm):
                dve.wait_ge(total_ready, norm + 1)
                nc.vector.tensor_scalar(var, ps[NT][:], 1.0 / D, EPS, ALU.mult, ALU.add).then_inc(var_ready, 1)

            def reciprocal_root(norm):
                dve.wait_ge(root_ready, norm + 1)
                nc.vector.reciprocal(rstd_b[:], root).then_inc(newton, 1)

            def newton_step(norm):
                r = rstd_b[:]
                dve.wait_ge(newton, 4 * norm + 1)
                link(nc.vector.scalar_tensor_tensor(out=root, in0=r, scalar=-0.5, in1=r, op0=ALU.mult,
                                                    op1=ALU.mult), newton, 4 * norm + 2)
                link(nc.vector.tensor_tensor(root, root, var, ALU.mult), newton, 4 * norm + 3)
                link(nc.vector.scalar_tensor_tensor(out=r, in0=root, scalar=1.5, in1=r, op0=ALU.add,
                                                    op1=ALU.mult), newton, 4 * norm + 4)

            def take_c(b, i, bk, q):
                nc.vector.tensor_tensor(u_pad[:, i, CW - 1:], bk, rstd_b[:], ALU.mult).then_inc(bank_free, 1)

            def take_v(b, i, bk, q):
                link(nc.vector.tensor_tensor(tmp[:, 0, :], bk, rstd_b[:], ALU.mult), bank_free, NT * b + (i + 1))
                link(nc.vector.tensor_tensor(u_pad[:, i, CW - 1:], u_pad[:, i, CW - 1:], tmp[:, 0, :], ALU.mult),
                     u_ready, NT * q + (i + 1))

            def split_z(value, idx, on, count, ready):
                link(nc.vector.tensor_copy(z_hi[:, bass.ds(idx, 1), :], value), on, count)
                link(nc.vector.tensor_tensor(z_lo[:, bass.ds(idx, 1), :], value,
                                             z_hi[:, bass.ds(idx, 1), :].bitcast(F32), ALU.subtract), z_ready, ready)

            def take_b(b, i, bk, q):
                done = 5 * NT * q + 5 * i
                t, y = tmp[:, 0, :], tmp[:, 1, :]

                def taps(j):
                    return cols[:, bass.ds(NT * q + ((2 + j) * DT + i), 1)]

                link(nc.vector.tensor_tensor(t, bk, rstd_b[:], ALU.mult), bank_free, NT * b + (i + 1))
                link(nc.vector.tensor_scalar(y, u_pad[:, i, 0:S], taps(0), None, ALU.mult), conv_step, done + 1)
                for j in (1, 2):
                    link(nc.vector.scalar_tensor_tensor(out=y, in0=u_pad[:, i, j:j + S], scalar=taps(j), in1=y,
                                                        op0=ALU.mult, op1=ALU.add), conv_step, done + (1 + j))
                link(nc.vector.tensor_tensor(y, y, t, ALU.mult), conv_step, done + 4)
                split_z(tmp[:, 1:2, :], NT * q + i, conv_step, done + 5, NT * q + (i + 1))

            def take_up(b, i, bk, c, j):
                done = 2 * KT * c + (2 * NT * j + 2 * i)
                link(nc.vector.tensor_tensor(tmp[:, 0, :], bk, rstd_b[:], ALU.mult), bank_free, NT * b + (i + 1))
                link(nc.vector.scalar_tensor_tensor(out=tmp[:, 1, :], in0=tmp[:, 0, :], scalar=0.0, in1=tmp[:, 0, :],
                                                    op0=ALU.max, op1=ALU.mult), relu_step, done + 1)
                split_z(tmp[:, 1:2, :], NT * j + i, relu_step, done + 2, KT * c + (NT * j + (KT + i + 1)))

            def take_resid(i, bk, n):
                at = resid[:, bass.ds(NT * n + i, 1), :].rearrange("p a t -> p (a t)")
                nc.vector.tensor_tensor(at, bk, at, ALU.add).then_inc(bank_free, 1)

            def block_step(b, parity, take):
                for k in range(KT):
                    split_lo(b + 1, k)
                    if k in TAKE_AT:
                        i = TAKE_AT.index(k)
                        if i == 0:
                            dve.wait_ge(w_used, KT * (b + 1))
                        take(i, ps[NT * parity + i][:])

            nc.vector.memset(u_pad[:, :, 0:CW - 1], 0.0).then_inc(pad_ready, 1)
            dve.wait_ge(pad_ready, 1)

            for k in range(KT):
                h_part(k, MIX)
                split_lo(0, k)
                for kk in SQUARES_AT.get(k, ()):
                    if kk > 0:
                        add_square(kk, 0)
                if k == 12:
                    variance(0)
                if k == 14:
                    reciprocal_root(0)
            newton_step(0)

            with dve.Fori(0, NQ // 2) as two:
                for sub in range(2):
                    for t, take in enumerate((take_c, take_v, take_b)):
                        q = 2 * two + sub
                        b = 6 * two + (3 * sub + t)
                        block_step(b, (3 * sub + t) % 2, lambda i, bk: take(b, i, bk, q))

            for n in range(NQ):
                b = OUT0 + n
                last = n == NQ - 1
                for k in range(KT):
                    split_lo(b + 1, k)
                    if k == 4:
                        dve.wait_ge(w_used, KT * (b + 1))
                    if 0 <= k - 4 < NT:
                        take_resid(k - 4, ps[NT * (b % 2) + k - 4][:], n)
                    i = k - 7
                    if 0 <= i < NT:
                        h_part(NT * n + i, MLP)
                        if NT * n + i > 0:
                            add_square(NT * n + i, 1)
                    if last and k == 12:
                        variance(1)
                    if last and k == 14:
                        reciprocal_root(1)
            newton_step(1)

            def up_pair(c, half):
                for sub in range(2):
                    j = 2 * half + sub
                    b = 2 * NQ * c + (2 * half + (MLP0 + sub))
                    block_step(b, sub, lambda i, bk: take_up(b, i, bk, c, j))

            def down_step(c, n, sub):
                b = 2 * NQ * c + (n + (MLP0 + NQ))
                block_step(b, sub, lambda i, bk: take_resid(i, bk, n))

            def down_pair(c, half):
                for sub in range(2):
                    down_step(c, 2 * half + sub, sub)

            with dve.Fori(0, NC - 1) as c:
                with dve.Fori(0, NQ // 2) as half:
                    up_pair(c, half)
                with dve.Fori(0, NQ // 2) as half:
                    down_pair(c, half)
            with dve.Fori(0, NQ // 2) as half:
                up_pair(NC - 1, half)
            down_pair(NC - 1, 0)
            down_step(NC - 1, NQ - 2, 0)
            for i in range(NT):
                dve.wait_ge(last_tile, i + 1)
                take_resid(i, ps[NT + i][:], NQ - 1)

        @block.tensor
        def _(pe):
            def pe_loop(start, end):
                return nc.Fori(start, end, engines=[mybir.EngineType.PE], hint_back_edge=True)

            H, Z = (h_hi, h_lo), (z_hi, z_lo)

            def tile_products(k, i, parity, act):
                whi, wlo = (w[:, k % RING, P * i:P * (i + 1)] for w in (w_hi, w_lo))
                hi, lo = (a[:, k, :] for a in act)
                for j, (stationary, moving) in enumerate(((wlo, hi), (whi, lo), (whi, hi))):
                    mm = nc.tensor.matmul(ps[NT * parity + i][:], stationary, moving, start=(k == 0 and j == 0),
                                          stop=(k == KT - 1 and j == 2))
                return mm

            def products(b, k, parity, act):
                pe.wait_ge(w_lo_ready, KT * b + (k + 1))
                for i in range(NT):
                    mm = tile_products(k, i, parity, act)
                mm.then_inc(w_used, 1)

            def banks_free(b):
                pe.wait_ge(bank_free, NT * (b - 1))

            def whole_block(b, parity, act):
                banks_free(b)
                for k in range(KT):
                    products(b, k, parity, act)

            def total(norm):
                pe.wait_ge(square_added, (DT - 1) * (norm + 1))
                nc.tensor.matmul(ps[NT][:], ones[:], square_sum, start=True, stop=True).then_inc(total_ready, 1)

            pe.wait_ge(ones_ready, 1)
            pe.wait_ge(h_hi_ready, 1)
            pe.wait_ge(w_hi_ready, 1)
            for i in range(NT):
                nc.tensor.matmul(ps[i][:], w_hi[:, 0, P * i:P * (i + 1)], h_hi[:, 0, :], start=True, stop=False)
            pe.wait_ge(h_lo_ready, 1)
            for i in range(NT):
                nc.tensor.matmul(ps[i][:], w_hi[:, 0, P * i:P * (i + 1)], h_lo[:, 0, :], start=False, stop=False)
            pe.wait_ge(w_lo_ready, 1)
            for i in range(NT):
                mm = nc.tensor.matmul(ps[i][:], w_lo[:, 0, P * i:P * (i + 1)], h_hi[:, 0, :], start=False, stop=False)
            mm.then_inc(w_used, 1)
            for k in range(1, KT):
                pe.wait_ge(h_lo_ready, k + 1)
                products(0, k, 0, H)
                if k == KT - 5:
                    total(0)
            pe.wait_ge(var_ready, 1)
            for k in range(KT):
                products(1, k, 1, H)
            with pe_loop(1, OUT0 // 2) as two:
                for sub in range(2):
                    whole_block(2 * two + sub, sub, H)

            with pe_loop(OUT0 // 2, MLP0 // 2) as two:
                for sub in range(2):
                    banks_free(2 * two + sub)
                    for k in range(KT):
                        if sub == 0:
                            pe.wait_ge(z_ready, k + 1)
                        products(2 * two + sub, k, sub, Z)

            banks_free(MLP0)
            for k in range(KT):
                pe.wait_ge(h_lo_ready, DT + k + 1)
                products(MLP0, k, 0, H)
                if k == KT - 5:
                    pe.wait_ge(bank_free, NT * MLP0)
                    total(1)
            pe.wait_ge(var_ready, 2)
            whole_block(MLP0 + 1, 1, H)

            def up_half(c, half):
                for sub in range(2):
                    whole_block(2 * NQ * c + (2 * half + (MLP0 + sub)), sub, H)

            def down_half(c, half):
                for sub in range(2):
                    b = 2 * NQ * c + (2 * half + (MLP0 + NQ + sub))
                    banks_free(b)
                    for k in range(KT):
                        if sub == 0:
                            pe.wait_ge(z_ready, KT * (c + 1) + (k + 1))
                        products(b, k, sub, Z)

            up_half(0, 1)
            with pe_loop(0, NC - 1) as c:
                with pe_loop(0, NQ // 2) as half:
                    down_half(c, half)
                with pe_loop(0, NQ // 2) as half:
                    up_half(c + 1, half)
            down_half(NC - 1, 0)
            whole_block(NB - 2, 0, Z)

            banks_free(NB - 1)
            for k in range(KT - 2):
                products(NB - 1, k, 1, Z)
            pe.wait_ge(w_lo_ready, KT * NB)
            for i in range(NT):
                for k in range(KT - 2, KT):
                    mm = tile_products(k, i, 1, Z)
                mm.then_inc(last_tile, 1)


def kernel(x, mix_norm, mlp_norm, mlp_w1, mlp_w2, conv_w_in, conv_w, conv_w_out, **unused):
    import numpy as _np
    import concourse.bacc as _bacc
    from concourse.bass_utils import run_bass_kernel_spmd as _run

    _, S, D = x.shape
    FF = mlp_w1.shape[2]
    NQ = D // BW

    def blocks(w, order):
        w = _np.asarray(w)[0]
        rows, columns = w.shape
        w = w.reshape(rows // D, NG, GRAN, P, columns // BW, BW)[:, :, :, :, order]
        return w.transpose(0, 4, 1, 3, 2, 5).reshape(-1, P, GRAN, BW)

    w_in = blocks(conv_w_in, [NQ * part + q for q in range(NQ) for part in (1, 2, 0)])
    w_out = blocks(conv_w_out, list(range(NQ)))
    up = blocks(mlp_w1, list(range(FF // BW))).reshape(FF // D, NQ * NG, P, GRAN, BW)
    down = blocks(mlp_w2, list(range(NQ))).reshape(FF // D, NQ * NG, P, GRAN, BW)
    mlp = _np.concatenate([up, down], axis=1).reshape(-1, P, GRAN, BW)
    stream = _np.concatenate([w_in, w_out, mlp], axis=0)
    rows = _np.concatenate([_np.asarray(mix_norm), _np.asarray(mlp_norm), _np.asarray(conv_w)[0]], axis=0)
    cols = _np.ascontiguousarray(rows.reshape(-1, P).T)
    xt = _np.ascontiguousarray(_np.asarray(x)[0].T)

    nc = _bacc.Bacc("TRN2", target_bir_lowering=False, num_devices=1)
    arrays = {"xt": xt, "weights": stream, "cols": cols}
    args = [nc.dram_tensor(f"in_{n}", a.shape, F32, kind="ExternalInput").ap() for n, a in arrays.items()]
    out = nc.dram_tensor("out", xt.shape, F32, kind="ExternalOutput").ap()
    conv_mlp_layer(nc, *args, out, FF)
    r = _run(nc, [{f"in_{n}": a for n, a in arrays.items()}], core_ids=[0])
    return _np.ascontiguousarray(r.results[0]["out"].T).reshape(x.shape)
```
